# Optimizing a Trainium2 kernel written in Bass

```python
import math
import jax, jax.numpy as jnp
from jax import lax
import numpy as np

D_MODEL = 1024
BATCH = 1
SEQ = 512
DEPTH = 2

D_MIX = 1024
HEAD_DIM = 64
N_ATTN_HEADS = 8
ATTN_WIDTH = N_ATTN_HEADS * HEAD_DIM
N_KV_HEADS = 2
GQA_REP = N_ATTN_HEADS // N_KV_HEADS
KV_W = N_KV_HEADS * HEAD_DIM
N_BRANCH = 3
CONV_WIDTH = D_MIX - ATTN_WIDTH
N_CONV_GROUPS = 8
CONV_K = 3
CMP_LEN = 32
CMP_STRIDE = 16
CMP_HIDDEN = 128
SEL_LEN = 64
SEL_TOPK = 16
WINDOW = 512
Q_BLOCK = 128
N_BUCKETS = 32
MAX_DISTANCE = 128
D_FF = 2816
N_EXPERTS = 8
TOP_K = 2
D_FF_EXPERT = 2816
EPS = 1e-6
NEG = -1e30
FORCE = 1e9
IN_COLS = ATTN_WIDTH + 6 * KV_W + N_BRANCH * N_ATTN_HEADS + 3 * CONV_WIDTH

kernel_name = "hymba_nsa_shortconv_moe_trunk"

def rms_norm(x, g):
    xf = x.astype(jnp.float32)
    y = xf * lax.rsqrt(jnp.mean(xf * xf, axis=-1, keepdims=True) + EPS)
    return (y * g.astype(jnp.float32)).astype(x.dtype)

def rel_bucket(dist):
    n = jnp.maximum(dist, 0)
    max_exact = N_BUCKETS // 2
    nf = jnp.maximum(n, max_exact).astype(jnp.float32)
    large = max_exact + (jnp.log(nf / max_exact) / math.log(MAX_DISTANCE / max_exact)
                         * (N_BUCKETS - max_exact)).astype(jnp.int32)
    large = jnp.minimum(large, N_BUCKETS - 1)
    return jnp.where(n < max_exact, n, large)

def masked_softmax(s, mask):
    s = jnp.where(mask, s, NEG)
    m = jnp.max(s, axis=-1, keepdims=True)
    e = jnp.exp(s - m) * mask
    return e / jnp.maximum(jnp.sum(e, axis=-1, keepdims=True), 1e-30)

def compress(kv, pos, w1, w2):
    B, S, G, dh = kv.shape
    n_cmp = (S - CMP_LEN) // CMP_STRIDE + 1
    idx = jnp.arange(n_cmp)[:, None] * CMP_STRIDE + jnp.arange(CMP_LEN)[None, :]
    blocks = kv[:, idx] + pos[None, None, :, None, :]
    flat = blocks.transpose(0, 1, 3, 2, 4).reshape(B, n_cmp, G, CMP_LEN * dh)
    return jax.nn.gelu(flat @ w1) @ w2

def nsa_attention(q, kc, vc, ks, vs, kw, vw, gates, rel_bias):
    B, S = q.shape[0], q.shape[1]
    G, R, dh, T = N_KV_HEADS, GQA_REP, HEAD_DIM, Q_BLOCK
    n_cmp = kc.shape[1]
    n_sel = S // SEL_LEN
    topk = min(SEL_TOPK, n_sel)
    scale = HEAD_DIM ** -0.5
    cmp_end = jnp.arange(n_cmp) * CMP_STRIDE + CMP_LEN - 1
    ks_blk = ks.reshape(B, n_sel, SEL_LEN, G, dh).transpose(0, 3, 1, 2, 4)
    vs_blk = vs.reshape(B, n_sel, SEL_LEN, G, dh).transpose(0, 3, 1, 2, 4)
    kw_pad = jnp.pad(kw, ((0, 0), (WINDOW, 0), (0, 0), (0, 0)))
    vw_pad = jnp.pad(vw, ((0, 0), (WINDOW, 0), (0, 0), (0, 0)))
    bias_gnr = rel_bias.reshape(N_BUCKETS, G, R).transpose(1, 0, 2)
    pad_l = CMP_LEN // CMP_STRIDE - 1
    ratio = SEL_LEN // CMP_STRIDE
    pad_r = ratio * n_sel - n_cmp
    gather = jax.vmap(jax.vmap(lambda kb, ib: kb[ib]))
    g_ar = jnp.arange(G)[None, :, None, None, None]

    def head_bias(dist):
        b = rel_bias[rel_bucket(dist)]
        return b.reshape(dist.shape[0], dist.shape[1], G, R).transpose(2, 3, 0, 1)[None].astype(jnp.float32)

    def block(c):
        t0 = c * T
        qg = lax.dynamic_slice_in_dim(q, t0, T, axis=1).reshape(B, T, G, R, dh)
        gc = lax.dynamic_slice_in_dim(gates, t0, T, axis=1).reshape(B, T, G, R, N_BRANCH)
        tpos = t0 + jnp.arange(T)
        dist_c = tpos[:, None] - cmp_end[None, :]
        s = jnp.einsum('btgrd,bngd->bgrtn', qg, kc).astype(jnp.float32) * scale + head_bias(dist_c)
        p_cmp = masked_softmax(s, (dist_c >= 0)[None, None, None])
        o_cmp = jnp.einsum('bgrtn,bngd->btgrd', p_cmp.astype(vc.dtype), vc)
        imp = jnp.pad(p_cmp.sum(axis=2), ((0, 0), (0, 0), (0, 0), (pad_l, pad_r)))
        imp_sel = 0.0
        for m in range(ratio):
            for n in range(CMP_LEN // CMP_STRIDE):
                st = m - n + pad_l
                imp_sel = imp_sel + lax.slice_in_dim(imp, st, st + ratio * (n_sel - 1) + 1, stride=ratio, axis=3)
        cur = tpos // SEL_LEN
        j = jnp.arange(n_sel)[None, :]
        forced = (j == 0) | (j == cur[:, None]) | (j == cur[:, None] - 1)
        score = jnp.where(forced, FORCE, imp_sel)
        score = jnp.where(j > cur[:, None], NEG, score)
        _, idx = lax.top_k(score, topk)
        blk_ok = idx <= cur[None, None, :, None]
        kg = gather(ks_blk, idx)
        vg = gather(vs_blk, idx)
        kpos = idx[..., None] * SEL_LEN + jnp.arange(SEL_LEN)
        dist_s = tpos[None, None, :, None, None] - kpos
        mask_s = blk_ok[..., None] & (dist_s >= 0)
        bias_s = jnp.moveaxis(bias_gnr[g_ar, rel_bucket(dist_s)], -1, 2).astype(jnp.float32)
        s = jnp.einsum('btgrd,bgtkld->bgrtkl', qg, kg).astype(jnp.float32) * scale + bias_s
        p = masked_softmax(s.reshape(B, G, R, T, topk * SEL_LEN),
                           mask_s.reshape(B, G, 1, T, topk * SEL_LEN)).reshape(s.shape)
        o_slc = jnp.einsum('bgrtkl,bgtkld->btgrd', p.astype(vg.dtype), vg)
        kwc = lax.dynamic_slice_in_dim(kw_pad, t0, T + WINDOW, axis=1)
        vwc = lax.dynamic_slice_in_dim(vw_pad, t0, T + WINDOW, axis=1)
        wpos = t0 - WINDOW + jnp.arange(T + WINDOW)
        dist_w = tpos[:, None] - wpos[None, :]
        mask_w = (dist_w >= 0) & (dist_w < WINDOW) & (wpos[None, :] >= 0)
        s = jnp.einsum('btgrd,bsgd->bgrts', qg, kwc).astype(jnp.float32) * scale + head_bias(dist_w)
        p = masked_softmax(s, mask_w[None, None, None])
        o_win = jnp.einsum('bgrts,bsgd->btgrd', p.astype(vwc.dtype), vwc)
        o = gc[..., 0:1] * o_cmp + gc[..., 1:2] * o_slc + gc[..., 2:3] * o_win
        return o.reshape(B, T, ATTN_WIDTH)

    out = lax.map(block, jnp.arange(S // T))
    return out.transpose(1, 0, 2, 3).reshape(B, S, ATTN_WIDTH)

def short_conv(bg, cg, hin, w):
    z = cg * hin
    y = lax.conv_general_dilated(z, w[:, None, :].astype(z.dtype), window_strides=(1,),
                                 padding=[(CONV_K - 1, 0)],
                                 dimension_numbers=('NWC', 'WIO', 'NWC'),
                                 feature_group_count=CONV_WIDTH)
    return bg * y

def swiglu(h, wg, wu, wd):
    return (jax.nn.silu(h @ wg) * (h @ wu)) @ wd

def moe_swiglu(h, router_w, router_b, wg, wu, wd):
    B, S, D = h.shape
    ht = h.reshape(-1, D)
    n_tok = ht.shape[0]
    logits = (ht @ router_w).astype(jnp.float32) + router_b.astype(jnp.float32)
    top_logit, top_idx = lax.top_k(logits, TOP_K)
    weights = jax.nn.softmax(top_logit, axis=-1)
    flat_e = top_idx.reshape(-1)
    flat_tok = jnp.repeat(jnp.arange(n_tok), TOP_K)
    order = jnp.argsort(flat_e)
    tok_sorted = flat_tok[order]
    xs = ht[tok_sorted]
    group_sizes = jnp.bincount(flat_e, length=N_EXPERTS).astype(jnp.int32)
    a = lax.ragged_dot(xs, wg, group_sizes)
    u = lax.ragged_dot(xs, wu, group_sizes)
    y = lax.ragged_dot(jax.nn.silu(a) * u, wd, group_sizes)
    y = y * weights.reshape(-1)[order][:, None].astype(y.dtype)
    out = jnp.zeros_like(ht).at[tok_sorted].add(y)
    return out.reshape(B, S, D)

def setup_inputs(seed: int = 0) -> dict:
    key = jax.random.key(seed)
    ks = jax.random.split(key, 32)
    f32 = jnp.float32
    n_dense = (DEPTH + 1) // 2
    n_moe = DEPTH // 2
    nrm = lambda k, shape, s: jax.random.normal(k, shape, f32) * s
    gain = lambda k, shape: 1.0 + 0.02 * jax.random.normal(k, shape, f32)
    return {
        "x": jax.random.normal(ks[0], (BATCH, SEQ, D_MODEL), f32),
        "rel_bias": nrm(ks[1], (N_BUCKETS, N_ATTN_HEADS), 0.5),
        "norm1": gain(ks[2], (DEPTH, D_MODEL)),
        "w_in": nrm(ks[3], (DEPTH, D_MODEL, IN_COLS), D_MODEL ** -0.5),
        "q_norm": gain(ks[4], (DEPTH, HEAD_DIM)),
        "k_norm": gain(ks[5], (DEPTH, N_BRANCH, HEAD_DIM)),
        "cmp_pos_k": nrm(ks[6], (DEPTH, CMP_LEN, HEAD_DIM), 0.1),
        "cmp_pos_v": nrm(ks[7], (DEPTH, CMP_LEN, HEAD_DIM), 0.1),
        "cmp_k_w1": nrm(ks[8], (DEPTH, CMP_LEN * HEAD_DIM, CMP_HIDDEN), (CMP_LEN * HEAD_DIM) ** -0.5),
        "cmp_k_w2": nrm(ks[9], (DEPTH, CMP_HIDDEN, HEAD_DIM), CMP_HIDDEN ** -0.5),
        "cmp_v_w1": nrm(ks[10], (DEPTH, CMP_LEN * HEAD_DIM, CMP_HIDDEN), (CMP_LEN * HEAD_DIM) ** -0.5),
        "cmp_v_w2": nrm(ks[11], (DEPTH, CMP_HIDDEN, HEAD_DIM), CMP_HIDDEN ** -0.5),
        "conv_w": nrm(ks[12], (DEPTH, CONV_K, CONV_WIDTH), CONV_K ** -0.5),
        "attn_out_norm": gain(ks[13], (DEPTH, ATTN_WIDTH)),
        "conv_out_norm": gain(ks[14], (DEPTH, CONV_WIDTH)),
        "w_out": nrm(ks[15], (DEPTH, D_MIX, D_MODEL), D_MIX ** -0.5),
        "norm2": gain(ks[16], (DEPTH, D_MODEL)),
        "ffn_w_gate": nrm(ks[17], (n_dense, D_MODEL, D_FF), D_MODEL ** -0.5),
        "ffn_w_up": nrm(ks[18], (n_dense, D_MODEL, D_FF), D_MODEL ** -0.5),
        "ffn_w_down": nrm(ks[19], (n_dense, D_FF, D_MODEL), D_FF ** -0.5),
        "router_w": nrm(ks[20], (n_moe, D_MODEL, N_EXPERTS), D_MODEL ** -0.5),
        "router_b": nrm(ks[21], (n_moe, N_EXPERTS), 0.01),
        "moe_w_gate": nrm(ks[22], (n_moe, N_EXPERTS, D_MODEL, D_FF_EXPERT), D_MODEL ** -0.5),
        "moe_w_up": nrm(ks[23], (n_moe, N_EXPERTS, D_MODEL, D_FF_EXPERT), D_MODEL ** -0.5),
        "moe_w_down": nrm(ks[24], (n_moe, N_EXPERTS, D_FF_EXPERT, D_MODEL), D_FF_EXPERT ** -0.5),
    }

def reference(x, rel_bias, norm1, w_in, q_norm, k_norm, cmp_pos_k, cmp_pos_v, cmp_k_w1, cmp_k_w2,
              cmp_v_w1, cmp_v_w2, conv_w, attn_out_norm, conv_out_norm, w_out, norm2,
              ffn_w_gate, ffn_w_up, ffn_w_down, router_w, router_b, moe_w_gate, moe_w_up, moe_w_down):
    B, S, _ = x.shape
    G, H, dh = N_KV_HEADS, N_ATTN_HEADS, HEAD_DIM
    sizes = [ATTN_WIDTH] + [KV_W] * 6 + [N_BRANCH * H] + [CONV_WIDTH] * 3
    split_at = [int(v) for v in np.cumsum(sizes)[:-1]]
    for layer in range(DEPTH):
        h = rms_norm(x, norm1[layer])
        proj = h @ w_in[layer]
        q, kc, vc, ksl, vsl, kwn, vwn, gts, cb, cc, ch = jnp.split(proj, split_at, axis=-1)
        q = rms_norm(q.reshape(B, S, H, dh), q_norm[layer])
        kc = rms_norm(compress(kc.reshape(B, S, G, dh), cmp_pos_k[layer], cmp_k_w1[layer], cmp_k_w2[layer]),
                      k_norm[layer, 0])
        vc = compress(vc.reshape(B, S, G, dh), cmp_pos_v[layer], cmp_v_w1[layer], cmp_v_w2[layer])
        ksl = rms_norm(ksl.reshape(B, S, G, dh), k_norm[layer, 1])
        kwn = rms_norm(kwn.reshape(B, S, G, dh), k_norm[layer, 2])
        gts = jax.nn.sigmoid(gts.reshape(B, S, H, N_BRANCH))
        o_attn = nsa_attention(q, kc, vc, ksl, vsl.reshape(B, S, G, dh), kwn,
                               vwn.reshape(B, S, G, dh), gts, rel_bias)
        o_conv = short_conv(cb, cc, ch, conv_w[layer])
        mixed = jnp.concatenate([rms_norm(o_attn, attn_out_norm[layer]),
                                 rms_norm(o_conv, conv_out_norm[layer])], axis=-1)
        x = x + mixed @ w_out[layer]
        h = rms_norm(x, norm2[layer])
        if layer % 2 == 0:
            i = layer // 2
            x = x + swiglu(h, ffn_w_gate[i], ffn_w_up[i], ffn_w_down[i])
        else:
            i = layer // 2
            x = x + moe_swiglu(h, router_w[i], router_b[i], moe_w_gate[i], moe_w_up[i], moe_w_down[i])
    return x


_drawn_inputs = setup_inputs


def setup_inputs(seed=0):
    import zlib

    import numpy as np

    out = dict(_drawn_inputs(seed))
    spreads = {}
    factors = {'q_norm': 3.732, 'k_norm': 3.526, 'router_b': 6.147}
    for name, (base, spread) in spreads.items():
        noise = np.random.default_rng([zlib.crc32(name.encode()), seed]).standard_normal(out[name].shape)
        drawn = base * np.exp(spread * noise) if base else spread * noise
        out[name] = __import__('jax').numpy.asarray(drawn.astype(out[name].dtype))
    for name, factor in factors.items():
        out[name] = (out[name] * factor).astype(out[name].dtype)
    return out
```

```python
import math
from contextlib import ExitStack

import numpy as np
import concourse.bass as bass
from concourse import mybir

F32 = mybir.dt.float32
I32 = mybir.dt.int32
U32 = mybir.dt.uint32
ALU = mybir.AluOpType
ACT = mybir.ActivationFunctionType
AX = mybir.AxisListType.X

P = 128
D = 1024
S = 512
DEPTH = 2
H, G, R, DH = 8, 2, 4, 64
TT = S // P
KD = D // P
CW = 512
CT = CW // P
NCMP = 31
HID = 128
LP = 16
NBUCKET = 32
FF = 2816
FT = FF // P
NSLOT = FT // 2
E = 8
CAP = 176
CB = CAP - P
CHUNKS = -(-S // CAP)
WIDTHS = (P, 136, 144, 160, CAP)
MAXR = E + (2 * S - E) // CAP
EPS = 1e-6
NEG = -1e30
ZLEN = 640

SLOT = 3 * KD * P
A_CV = 0
A_Q = CT * SLOT
A_KV = A_Q + KD * 512
A_KC = A_KV + KD * 512
KCW = 2 * 128 + 24
A_QT = A_KC + KD * KCW
A_KT = A_QT + 4 * S
A_V = A_KT + 4 * S
A_MIX = A_V + TT * 256
A_Z = A_MIX + KD * S
A_END = A_Z + 2 * G * 256
ARENA = NSLOT * SLOT
A_T = A_Q
A_W1 = A_KV
A_WO = CT * SLOT - KD * D
assert A_END <= ARENA and A_WO >= SLOT

C_ID, C_ONE, C_TRI, C_IOTA = 0, P, 2 * P, 3 * P
C_TOK = C_IOTA + CAP
C_I8 = C_TOK + TT
C_HALF = C_I8 + E
C_VALID = C_HALF + 4 * MAXR
C_EXP = C_VALID + 1
C_END = C_EXP + 8

B_AN, B_QN, B_KN, B_END = 0, 512, 576, 576 + 3 * DH
PC_CONV, PC_CN, PC_POS, PC_W2 = 0, 3 * CT, 4 * CT, 4 * CT + 2 * LP
PC_END = PC_W2 + 2 * DH


def bc_last(ap, n):
    shape = list(ap.shape)
    return ap.unsqueeze(len(shape)).to_broadcast(shape + [n])


def bc_mid(ap, at, n):
    shape = list(ap.shape)
    return ap.unsqueeze(at).to_broadcast(shape[:at] + [n] + shape[at:])


def build(nc, x_in, table, onehot, const, w_q, w_kv, w_kc, w_cv, w_1, w_o, n_b, p_b, p_c, f_gu, f_dn,
          r_w, r_b, m_w, out):
    ctx = ExitStack()
    with ctx:
        def sb(name, shape, dt=F32):
            return ctx.enter_context(nc.sbuf_tensor(name, shape, dt))

        def sem(name):
            return ctx.enter_context(nc.semaphore(name))

        bias_dram = nc.dram_tensor("bias_by_distance", [H, ZLEN], F32)
        shifted_dram = nc.dram_tensor("bias_by_query_and_key", [H, P, S], F32)
        h_dram = nc.dram_tensor("normed_tokens", [S, D], F32)
        y_dram = nc.dram_tensor("expert_rows", [MAXR * CAP, D], F32)

        ps = ctx.enter_context(nc.psum_tensor("ps", [P, 8, 512], F32))
        arena = sb("arena", [P, ARENA])
        x = sb("x", [P, TT, D])
        hT = sb("hT", [P, KD, S])
        gb = sb("gb", [P, D])
        work = sb("work", [P, 6 * S])
        w2 = work[:, :].rearrange("p (a b n) -> p a b n", a=3, b=2)
        sb_s, sb_p, sb_pt = w2[:, 0], w2[:, 1], w2[:, 2]
        xn = work[:, 0:2 * D].rearrange("p (a n) -> p a n", a=2)
        junk = work[:, 2 * D:3 * D]
        yc, sqsum, sqb = sb_s[:, 0, :], sb_s[:, 1, :], sb_p[:, 0, :]
        zc = sb("zc", [P, S + 2])
        ccb = sb("ccb", [P, S])
        qk = sb("qk", [P, 2, S])
        qn, kn = qk[:, 0, :], qk[:, 1, :]
        table_sb = sb("table_sb", [33, H])
        oh_sb = arena[0:33, A_MIX:A_MIX + ZLEN]
        bias_row = arena[0:H, A_MIX + D:A_MIX + D + ZLEN]
        cst = sb("cst", [P, C_END])
        pb = sb("pb", [P, B_END])
        pc = sb("pc", [P, PC_END])
        st = sb("st", [P, 256])
        kcT = sb("kcT", [P, G, 32])
        vbd = sb("vbd", [P, G, 256])
        hidc = sb("hidc", [P, 2, 2 * NCMP])
        gts = sb("gts", [P, TT, H, 3])

        cv_w = [arena[:, A_CV + c * SLOT:A_CV + (c + 1) * SLOT].rearrange("p (k n) -> p k n", k=KD) for c in range(CT)]
        q_w = arena[:, A_Q:A_KV].rearrange("p (k n) -> p k n", k=KD)
        kv_w = arena[:, A_KV:A_KC].rearrange("p (k n) -> p k n", k=KD)
        kc_w = arena[:, A_KC:A_QT].rearrange("p (k n) -> p k n", k=KD)
        qT = arena[:, A_QT:A_KT].rearrange("p (k n) -> p k n", k=4)
        kT = arena[:, A_KT:A_V].rearrange("p (k n) -> p k n", k=4)
        V = arena[:, A_V:A_MIX].rearrange("p (t n) -> p t n", t=TT)
        mixT = arena[:, A_MIX:A_Z].rearrange("p (k n) -> p k n", k=KD)
        Z = arena[:, A_Z:A_END].rearrange("p (a g n) -> p a g n", a=2, g=G)
        T = arena[:, A_T:A_T + H * S].rearrange("p (h n) -> p h n", h=H)
        W1 = arena[:, A_W1:A_W1 + 2 * LP * HID].rearrange("p (a l n) -> p a l n", a=2, l=LP)
        WO = arena[:, A_WO:A_WO + KD * D].rearrange("p (k n) -> p k n", k=KD)
        slot = [arena[:, s * SLOT:(s + 1) * SLOT] for s in range(NSLOT)]
        gate_w = [a[:, 0:KD * P].rearrange("p (k n) -> p k n", k=KD) for a in slot]
        up_w = [a[:, KD * P:2 * KD * P].rearrange("p (k n) -> p k n", k=KD) for a in slot]
        down_w = [a[:, 2 * KD * P:SLOT] for a in slot]
        ident = cst[:, C_ID:C_ID + P]
        ones = cst[:, C_ONE:C_ONE + P]
        tri = cst[:, C_TRI:C_TRI + P]

        ss = st[:, 0:4]
        rstd = st[:, 4:8]
        ssh = st[:, 8:16]
        rh = st[:, 16:24]
        ssa = st[:, 24:28]
        ra = st[:, 28:32]
        rc = st[:, 32:36]
        posb = st[:, 36:38]
        den = [st[:, 40 + 64 * i:64 + 64 * i].rearrange("p (b h) -> p b h", b=3) for i in range(2)]
        coef = st[:, 64:88].rearrange("p (b h) -> p b h", b=3)
        negm = st[:, 88:104]
        cmx = st[:, 104:112]
        Sc = sb("Sc", [P, H, 32])
        Pc = sb("Pc", [P, H, 32])
        PcT = sb("PcT", [P, G, P])
        on = qn
        on_t = kn

        x_in_s = [sem(f"x_in{t}") for t in range(TT)]
        const_in = sem("const_in")
        table_in = sem("table_in")
        params_in = sem("params_in")
        gain_in = sem("gain_in")
        wq_in, wkv_in, wkc_in = sem("wq_in"), sem("wkv_in"), sem("wkc_in")
        wcv_in = [sem(f"wcv_in{c}") for c in range(CT)]
        w1_in, wo_in, T_in = sem("w1_in"), sem("wo_in"), sem("T_in")
        slot_in = [sem(f"slot_in{s}") for s in range(NSLOT)]
        bias_stored, spare_rows = sem("bias_stored"), sem("spare_rows")
        power_in, power_out = sem("power_in"), sem("power_out")
        bias_ps, bias_sb, bias_out = sem("bias_ps"), sem("bias_sb"), sem("bias_out")
        zeroed = sem("zeroed")
        ss_done, xn_done, xt_done = sem("ss_done"), sem("xn_done"), sem("xt_done")
        hta, htd = sem("ht_by_act"), sem("ht_by_dve")
        dch = sem("dve_chain")
        ach = sem("act_chain")
        pq_done, pkv_done, pkc_done, pcv_done = sem("pq_done"), sem("pkv_done"), sem("pkc_done"), sem("pcv_done")
        sq_done, red_done = sem("sq_done"), sem("red_done")
        qn_done, kn_done = sem("qn_done"), sem("kn_done")
        qt_ps, kt_ps = sem("qt_ps"), sem("kt_ps")
        qt_done, kt_done, v_done = sem("qt_done"), sem("kt_done"), sem("v_done")
        z_done, gexp_done, gate_done = sem("z_done"), sem("gexp_done"), sem("gate_done")
        hp_done, pos_done, gelu_done, ho_done = sem("hp_done"), sem("pos_done"), sem("gelu_done"), sem("ho_done")
        kcn_done, kct_ps, kct_done, vbd_done = sem("kcn_done"), sem("kct_ps"), sem("kct_done"), sem("vbd_done")
        cc_done, cv_done, cvm_done, sqs_done = sem("cc_done"), sem("cv_done"), sem("cvm_done"), sem("sqs_done")
        cs_ps, rc_done = sem("cs_ps"), sem("rc_done")
        s_ps, sb_done, p_done, pt_ps, pta, ptd, o_ps = (sem("s_ps"), sem("scores_done"), sem("probs_done"),
            sem("pt_ps"), sem("pt_by_act"), sem("pt_by_dve"), sem("o_ps"))
        cs1_ps, csub_done, cp_done, cpt_ps, cpt_done, co_ps = (sem("cmp_scores_ps"), sem("cmp_scores_done"),
            sem("cmp_probs_done"), sem("cmp_pt_ps"), sem("cmp_pt_done"), sem("cmp_o_ps"))
        o_read = sem("o_read")
        comb_done, ssa_done, og_done, ot_ps, ot_done = (sem("comb_done"), sem("ssa_done"), sem("og_done"),
            sem("ot_ps"), sem("ot_done"))
        po_ps, xres = sem("po_ps"), sem("xres")
        fg_ps, fsg_done, fh_done, tile_used, fd_ps, xffn = (sem("ffn_ps"), sem("ffn_silu_done"), sem("ffn_hidden_done"),
            sem("tile_used"), sem("ffn_down_ps"), sem("xffn"))

        mm = nc.tensor.matmul
        tr = nc.tensor.transpose
        v = nc.vector
        act = nc.scalar.activation

        small = sb("small", [P, 512])
        iw = sb("iw", [P, 96], I32)
        cut = lambda t, a, *d: (t[:, a:a + int(np.prod(d))] if len(d) == 1 else
                                t[:, a:a + int(np.prod(d))].rearrange("p (a b) -> p a b", a=d[0]) if len(d) == 2 else
                                t[:, a:a + int(np.prod(d))].rearrange("p (a b c) -> p a b c", a=d[0], b=d[1]))
        rb = cut(small, 0, E)
        lg = cut(small, 8, TT, E)
        mx = cut(small, 40, TT, E)
        oh = cut(small, 72, 2, TT, E)
        msk = cut(small, 136, TT, E)
        ixf = cut(small, 168, TT, E)
        cnt = cut(small, 200, E)
        chn = cut(small, 208, E)
        rs = cut(small, 216, E + 1)
        rbase = cut(small, 226, E)
        posr = cut(small, 234, TT, E)
        tmpr = cut(small, 266, 2, TT, E)
        rowf = cut(small, 330, 2, TT)
        tile_f = cut(small, 338, 2 * MAXR)
        tile_t = cut(small, 364, 2 * MAXR)
        dm = cut(small, 390, TT)
        ew = cut(small, 394, TT)
        wts = cut(small, 398, 2, TT)
        ixu = cut(iw, 0, TT, E).bitcast(U32)
        rowi = cut(iw, 32, 2, TT)
        meta = iw[0:1, 40:40 + 2 * MAXR + 1]
        width_i = iw[0:1, 74:74 + MAXR]
        last_row = cut(small, 410, E)
        grow = cut(small, 418, E)
        left = cut(small, 426, MAXR)
        left_t = cut(small, 440, MAXR)
        idx = iw[:, 70:72]
        rw = sb("rw", [P, KD, E])
        hid = sb("hid", [P, 2, CAP])
        sg = sb("sg", [P, 2, CAP])
        pick = qk[:, :, :].rearrange("p a n -> p (a n)")[:, 0:TT * CAP].rearrange("p (t n) -> p t n", t=TT)
        pick1 = zc[:, 0:CAP]
        hflat = hT[:, :, :].rearrange("p k n -> p (k n)")
        xsA, xsB, ysA, ysB = (hflat[:, i * D:(i + 1) * D] for i in range(4))
        xT = work[:, 0:KD * CAP].rearrange("p (k n) -> p k n", k=KD)
        yT = work[:, KD * CAP:2 * KD * CAP].rearrange("p (k n) -> p k n", k=KD)

        router_in, h_out = sem("router_in"), [sem(f"h_out{i}") for i in range(2)]
        rl_ps, max_done, ew_done, mask_done, pos_ps, meta_done = (sem("router_ps"), sem("max_done"), sem("ew_done"),
            sem("mask_done"), sem("positions_ps"), sem("meta_done"))
        pick_done, ix_ps, ix_done, xs_in = sem("pick_done"), sem("index_ps"), sem("index_done"), sem("gathered")
        mp6, mp7, me6, me7 = sem("bank6_ps"), sem("bank7_ps"), sem("bank6_read"), sem("bank7_read")
        gu_ps, sg_done, hid_done, y_ps, ya, yd = (sem("gate_up_ps"), sem("silu_done"), sem("hidden_done"), sem("y_ps"),
            sem("y_by_act"), sem("y_by_dve"))
        y_out, fin_in, fin_done, out_s = sem("y_out"), [sem(f"fin_in{i}") for i in range(2)], sem("fin_done"), sem("out_stored")
        U0 = FT + NSLOT
        I0 = 48

        def rounds(eng):
            eng.wait_ge(meta_done, 1)
            return eng.value_load(meta[:, 2 * MAXR:2 * MAXR + 1], min_val=E, max_val=MAXR)

        def moe_loads(sp):
            for s in range(NSLOT):
                if s == 1:
                    sp.wait_ge(po_ps, TT * DEPTH)
                if s == 2:
                    for t in range(TT):
                        sp.wait_ge(xn_done, 12 + t + 1)
                        sp.dma_start(h_dram[t * P:(t + 1) * P, :], xn[:, t % 2, :]).then_inc(h_out[t % 2], 16)
                if s == 6:
                    sp.wait_ge(xs_in, 32)
                sp.dma_start(slot[s], m_w[s]).then_inc(slot_in[s], 16)
            n = rounds(sp)
            with sp.Fori(1, n * 2) as q:
                first = sp.value_load(meta[:, bass.ds(q, 1)], min_val=0, max_val=E * FT - NSLOT)
                for s in range(NSLOT):
                    sp.wait_ge(tile_used, (q - 1) * NSLOT + (U0 + s + 1))
                    sp.dma_start(slot[s], m_w[bass.ds(first + s, 1)].rearrange("o p n -> (o p) n")).then_inc(slot_in[s], 16)

        def moe_products(pe):
            pe.wait_ge(router_in, 32)
            for t in range(TT):
                for k in range(KD):
                    m = mm(ps[:, 0, E * t:E * (t + 1)], hT[:, k, t * P:(t + 1) * P], rw[:, k, :], start=(k == 0), stop=(k == KD - 1))
            m.then_inc(rl_ps, 1)
            pe.wait_ge(mask_done, 1)
            for t in range(TT + 1):
                for j in range(min(t + 1, TT)):
                    m = mm(ps[:, 1, E * t:E * (t + 1)], tri if j == t else ones, msk[:, j, :], start=(j == 0), stop=(j == min(t, TT - 1)))
            m.then_inc(pos_ps, 1)

            def index(n):
                pe.wait_ge(pick_done, n + 1)
                for j, (a, w) in enumerate(((0, P), (P, CB))):
                    for t in range(TT):
                        m = mm(ps[0:w, 7, 400 + 2 * j:401 + 2 * j], pick[:, t, a:a + w], cst[:, C_TOK + t:C_TOK + t + 1],
                               start=(t == 0), stop=(t == TT - 1))
                m.then_inc(ix_ps, 1)

            def turn_x(b, use):
                bank = 6 + b % 2
                pe.wait_ge(me7 if b % 2 else me6, use)
                for j in range(2):
                    k = 2 * b + j
                    tr(ps[:, bank, j * CAP:j * CAP + P], xsA[:, k * P:(k + 1) * P], ident)
                    m = tr(ps[:, bank, j * CAP + P:(j + 1) * CAP], xsB[0:CB, k * P:(k + 1) * P], ident[0:CB, 0:CB])
                m.then_inc(mp7 if b % 2 else mp6, 1)

            index(0)
            pe.wait_ge(ix_done, 1)
            pe.wait_ge(xs_in, 32)
            for b in range(4):
                turn_x(b, b // 2)
            n = rounds(pe)
            with pe.Fori(0, n) as r:
                wide = pe.value_load(width_i[:, bass.ds(r, 1)], min_val=0, max_val=len(WIDTHS) - 1)

                def gate_up(s, W):
                    pe.wait_ge(slot_in[s % NSLOT], r * 32 + (I0 + 16 * (s // NSLOT + 1)))
                    if s == 0:
                        pe.wait_ge(me6, r * 4 + 2)
                        pe.wait_ge(me7, r * 4 + 2)
                    pe.wait_ge(hid_done, r * FT + (s + 1))
                    for j, w in enumerate((gate_w[s % NSLOT], up_w[s % NSLOT])):
                        for k in range(KD):
                            m = mm(ps[:, s % 2, j * CAP:j * CAP + W], w[:, k, :], xT[:, k, 0:W], start=(k == 0), stop=(k == KD - 1))
                    m.then_inc(gu_ps, 1)

                def down(s, W):
                    pe.wait_ge(hid_done, r * FT + (s + 3))
                    if s == 0:
                        pe.wait_ge(ya, r * 2 + 2)
                        pe.wait_ge(yd, r * 2 + 2)
                    for j in range(KD):
                        m = mm(ps[:, 2 + j // 2, (j % 2) * CAP:(j % 2) * CAP + W], down_w[s % NSLOT][:, j * P:(j + 1) * P],
                               hid[:, s % 2, 0:W], start=(s == 0 and j % 2 == 0), stop=(s == FT - 1), skip_group_check=True)
                    m.then_inc(tile_used, 1)

                def products(W):
                    for s in range(FT):
                        gate_up(s, W)
                        if 0 < s < FT - 1:
                            down(s - 1, W)
                        if s == 10:
                            pe.wait_ge(me7, r * 4 + 4)
                            index(r + 1)
                    pe.wait_ge(xs_in, r * 32 + 64)
                    turn_x(0, r * 4 + 4)
                    turn_x(1, r * 4 + 4)
                    down(FT - 2, W)
                    down(FT - 1, W)

                for c, W in enumerate(WIDTHS):
                    with pe.If(wide == c):
                        products(W)
                pe.wait_ge(tile_used, r * FT + (U0 + FT))
                turn_x(2, r * 4 + 5)
                turn_x(3, r * 4 + 5)
                pe.wait_ge(ya, r * 2 + 4)
                pe.wait_ge(yd, r * 2 + 4)
                for a, w, use in ((0, P, 6), (P, CB, 7)):
                    for b in range(2):
                        free = pe.to_reg(r * 4 + use)
                        pe.wait_ge(const_in, 16)
                        pe.wait_ge(me7 if b else me6, free)
                        for k in range(4):
                            m = tr(ps[0:w, 6 + b, k * P:(k + 1) * P], yT[:, 4 * b + k, a:a + w], ident)
                        m.then_inc(mp7 if b else mp6, 1)

        def moe_vector(dve, after):
            dve.wait_ge(router_in, 32)
            dve.wait_ge(rl_ps, 1)
            after(v.tensor_tensor(lg, ps[:, 0, 0:TT * E].rearrange("p (t e) -> p t e", t=TT), bc_mid(rb, 1, TT), ALU.add))
            for t in range(TT):
                after(v.max(mx[:, t, :], lg[:, t, :]))
            for t in range(TT):
                m = v.max_index(ixu[:, t, :], mx[:, t, :], lg[:, t, :])
            after(m)
            v.tensor_tensor(dm, mx[:, :, 1], mx[:, :, 0], ALU.subtract).then_inc(max_done, 1)
            after(v.tensor_copy(ixf, ixu))
            for c in range(2):
                after(v.tensor_tensor(oh[:, c], bc_mid(cst[:, C_I8:C_I8 + E], 1, TT), bc_last(ixf[:, :, c], E), ALU.is_equal))
            v.tensor_tensor(msk, oh[:, 0], oh[:, 1], ALU.add).then_inc(mask_done, 1)
            dve.wait_ge(ew_done, 1)
            after(v.tensor_scalar(wts[:, 0, :], ew, 1.0, None, ALU.add))
            after(v.reciprocal(wts[:, 0, :], wts[:, 0, :]))
            after(v.tensor_tensor(wts[:, 1, :], wts[:, 0, :], ew, ALU.mult))
            dve.wait_ge(pos_ps, 1)
            after(v.tensor_copy(cnt, ps[:, 1, TT * E:(TT + 1) * E]))
            after(v.tensor_scalar(chn, cnt, float(CAP), 1.0, ALU.is_gt, ALU.add))
            for c in range(2, CHUNKS):
                after(v.scalar_tensor_tensor(chn, cnt, float(c * CAP), chn, ALU.is_gt, ALU.add))
            after(v.memset(rs[:, 0:1], 0.0))
            for e in range(E):
                after(v.tensor_tensor(rs[:, e + 1:e + 2], rs[:, e:e + 1], chn[:, e:e + 1], ALU.add))
            after(v.tensor_scalar(rbase, rs[:, 0:E], float(CAP), None, ALU.mult))
            after(v.tensor_tensor(posr, ps[:, 1, 0:TT * E].rearrange("p (t e) -> p t e", t=TT), bc_mid(rbase, 1, TT), ALU.add))
            for c in range(2):
                m = v.tensor_tensor(tmpr[:, c], oh[:, c], posr, ALU.mult)
            after(m)
            for c in range(2):
                m = v.tensor_reduce(rowf[:, c, :], tmpr[:, c], AX, ALU.add)
            after(m)
            after(v.tensor_copy(rowi, rowf))

            def picks():
                for t in range(TT):
                    after(v.tensor_scalar(pick1, cst[:, C_IOTA:C_IOTA + CAP], rowf[:, 0, t:t + 1], None, ALU.is_equal))
                    m = v.scalar_tensor_tensor(pick[:, t, :], cst[:, C_IOTA:C_IOTA + CAP], rowf[:, 1, t:t + 1], pick1, ALU.is_equal, ALU.add)
                    if t < TT - 1:
                        after(m)
                m.then_inc(pick_done, 1)

            def indices():
                v.tensor_copy(idx[:, 0:1], ps[:, 7, 400:401])
                v.tensor_copy(idx[0:CB, 1:2], ps[0:CB, 7, 402:403]).then_inc(ix_done, 1)

            def copy_x(b):
                v.tensor_copy(xT[:, 2 * b:2 * b + 2, :], ps[:, 7, 0:2 * CAP].rearrange("p (k n) -> p k n", k=2)).then_inc(me7, 1)

            picks()
            dve.wait_ge(ix_ps, 1)
            indices()
            after(v.tensor_copy(tile_f, cst[:, C_HALF + 2 * MAXR:C_HALF + 4 * MAXR]))
            for e in range(1, E):
                after(v.tensor_scalar(tile_t, cst[:, C_HALF:C_HALF + 2 * MAXR], rs[:, e:e + 1], float(FT), ALU.is_ge, ALU.mult))
                after(v.tensor_tensor(tile_f, tile_f, tile_t, ALU.add))
            after(v.tensor_tensor(last_row, rbase, cnt, ALU.add))
            after(v.tensor_tensor(grow[:, 1:E], last_row[:, 1:E], last_row[:, 0:E - 1], ALU.subtract))
            order = cst[:, C_IOTA:C_IOTA + MAXR]
            after(v.tensor_scalar(left, order, -float(CAP), last_row[:, 0:1], ALU.mult, ALU.add))
            for e in range(1, E):
                after(v.tensor_scalar(left_t, order, rs[:, e:e + 1], grow[:, e:e + 1], ALU.is_ge, ALU.mult))
                after(v.tensor_tensor(left, left, left_t, ALU.add))
            after(v.tensor_scalar(left_t, left, float(WIDTHS[0]), None, ALU.is_gt))
            for w in WIDTHS[1:-1]:
                after(v.scalar_tensor_tensor(left_t, left, float(w), left_t, ALU.is_gt, ALU.add))
            v.tensor_copy(width_i, left_t[0:1, :])
            v.tensor_copy(meta[:, 0:2 * MAXR], tile_f[0:1, :])
            v.tensor_copy(meta[:, 2 * MAXR:2 * MAXR + 1], rs[0:1, E:E + 1]).then_inc(meta_done, 1)
            for i in range(2):
                dve.wait_ge(h_out[i], 32)
            for b in (1, 3):
                dve.wait_ge(mp7, b // 2 + 1)
                copy_x(b)
            for i in range(2):
                v.memset(hid[:, i, :], 0.0).then_inc(hid_done, 1)
            for i in range(2):
                v.memset(ysB[0:CB, 512 * i:512 * i + 8], 0.0).then_inc(me7, 1)
                dve.sem_inc(yd, 1)
            n = rounds(dve)
            dve.wait_ge(pick_done, 1)
            base = moe_chain(dve)
            with dve.Fori(0, n) as r:
                for s in range(FT):
                    dve.wait_ge(sg_done, r * FT + (s + 1))
                    dve.wait_ge(tile_used, r * FT + (U0 + s - 1))
                    v.tensor_tensor(hid[:, s % 2, :], sg[:, s % 2, :], ps[:, s % 2, CAP:2 * CAP], ALU.mult).then_inc(hid_done, 1)
                    if s == 4:
                        dve.wait_ge(ix_ps, r + 1)
                        link = base(r)
                        link(v.tensor_scalar(rowf, rowf, -float(CAP), None, ALU.add))
                        for t in range(TT):
                            link(v.tensor_scalar(pick1, cst[:, C_IOTA:C_IOTA + CAP], rowf[:, 0, t:t + 1], None, ALU.is_equal))
                            m = v.scalar_tensor_tensor(pick[:, t, :], cst[:, C_IOTA:C_IOTA + CAP], rowf[:, 1, t:t + 1], pick1, ALU.is_equal, ALU.add)
                            if t < TT - 1:
                                link(m)
                        m.then_inc(pick_done, 1)
                    if s == 12:
                        dve.wait_ge(ix_ps, r + 2)
                        dve.wait_ge(xs_in, r * 32 + 32)
                        indices()
                dve.wait_ge(mp7, r * 4 + 3)
                copy_x(1)
                dve.wait_ge(tile_used, r * FT + (U0 + FT))
                for b in (2, 3):
                    v.tensor_copy(yT[:, 2 * b:2 * b + 2, :], ps[:, 2 + b, 0:2 * CAP].rearrange("p (k n) -> p k n", k=2)).then_inc(yd, 1)
                dve.wait_ge(mp7, r * 4 + 4)
                copy_x(3)
                dve.wait_ge(y_out, r * 32 + 32)
                dve.wait_ge(mp7, r * 4 + 5)
                v.tensor_copy(ysA[:, 512:D], ps[:, 7, :]).then_inc(me7, 1)
                dve.wait_ge(mp7, r * 4 + 6)
                v.tensor_copy(ysB[0:CB, 512:D], ps[0:CB, 7, :]).then_inc(me7, 1)
            for t in range(TT):
                dve.wait_ge(fin_in[t % 2], 32 * (t // 2 + 1))
                for c in range(2):
                    m = v.scalar_tensor_tensor(x[:, t, :], hflat[:, (2 * (t % 2) + c) * D:(2 * (t % 2) + c + 1) * D],
                                               wts[:, c, t:t + 1], x[:, t, :], ALU.mult, ALU.add)
                    if c == 0:
                        m.then_inc(fin_done, 1)
                        dve.wait_ge(fin_done, 2 * t + 1)
                m.then_inc(fin_done, 1)

        def moe_chain(dve):
            per = 1 + TT + TT - 1
            ch = sem("pick_chain")

            def base(r):
                k = [0]

                def link(ins):
                    k[0] += 1
                    ins.then_inc(ch, 1)
                    dve.wait_ge(ch, r * per + k[0])
                return link
            return base

        def moe_scalar(se):
            se.wait_ge(max_done, 1)
            act(ew, dm, ACT.Exp).then_inc(ew_done, 1)

            def copy_x(b):
                nc.scalar.copy(xT[:, 2 * b:2 * b + 2, :], ps[:, 6, 0:2 * CAP].rearrange("p (k n) -> p k n", k=2)).then_inc(me6, 1)

            for i in range(2):
                se.wait_ge(h_out[i], 32)
            for b in (0, 2):
                se.wait_ge(mp6, b // 2 + 1)
                copy_x(b)
            for i in range(2):
                nc.scalar.copy(ysA[0:1, 8 * i:8 * i + 8], cst[0:1, 0:8]).then_inc(me6, 1)
                se.sem_inc(ya, 1)
            n = rounds(se)
            with se.Fori(0, n) as r:
                for s in range(FT):
                    se.wait_ge(gu_ps, r * FT + (s + 1))
                    se.wait_ge(hid_done, r * FT + (s + 1))
                    act(sg[:, s % 2, :], ps[:, s % 2, 0:CAP], ACT.Silu).then_inc(sg_done, 1)
                se.wait_ge(mp6, r * 4 + 3)
                copy_x(0)
                se.wait_ge(tile_used, r * FT + (U0 + FT))
                for b in (0, 1):
                    nc.scalar.copy(yT[:, 2 * b:2 * b + 2, :], ps[:, 2 + b, 0:2 * CAP].rearrange("p (k n) -> p k n", k=2)).then_inc(ya, 1)
                se.wait_ge(mp6, r * 4 + 4)
                copy_x(2)
                se.wait_ge(y_out, r * 32 + 32)
                se.wait_ge(mp6, r * 4 + 5)
                nc.scalar.copy(ysA[:, 0:512], ps[:, 6, :]).then_inc(me6, 1)
                se.wait_ge(mp6, r * 4 + 6)
                nc.scalar.copy(ysB[0:CB, 0:512], ps[0:CB, 6, :]).then_inc(me6, 1)
                se.wait_ge(me6, r * 4 + 8)
                se.wait_ge(me7, r * 4 + 8)
                se.dma_start(y_dram[bass.ds(r * CAP, P), :], ysA).then_inc(y_out, 16)
                se.dma_start(y_dram[bass.ds(r * CAP + P, CB), :], ysB[0:CB, :]).then_inc(y_out, 16)
            se.wait_ge(y_out, n * 32 + 32)
            se.sem_inc(all_rows, 1)
            for t in range(TT):
                se.wait_ge(fin_done, 2 * t + 2)
                se.dma_start(out[t * P:(t + 1) * P, :], x[:, t, :]).then_inc(out_s, 16)
            se.wait_ge(out_s, 16 * TT)

        all_rows = sem("all_rows_stored")

        def moe_gathers(pool):
            pool.dma_start(rw[:, :, :], r_w).then_inc(router_in, 16)
            pool.dma_start(rb, r_b.to_broadcast([P, E])).then_inc(router_in, 16)

            def gather():
                pool.indirect_dma_start(xsA, None, h_dram[:, :], bass.IndirectOffsetOnAxis(ap=idx[:, 0:1], axis=0)).then_inc(xs_in, 16)
                pool.indirect_dma_start(xsB[0:CB, :], None, h_dram[:, :], bass.IndirectOffsetOnAxis(ap=idx[0:CB, 1:2], axis=0)).then_inc(xs_in, 16)

            for i in range(2):
                pool.wait_ge(h_out[i], 32)
            pool.wait_ge(rl_ps, 1)
            pool.wait_ge(ix_done, 1)
            gather()
            n = rounds(pool)
            with pool.Fori(0, n) as r:
                known = pool.to_reg(r + 2)
                pool.wait_ge(meta_done, 1)
                pool.wait_ge(ix_done, known)
                gather()
            pool.wait_ge(all_rows, 1)
            for t in range(TT):
                if t >= 2:
                    pool.wait_ge(fin_done, 2 * t - 2)
                for c in range(2):
                    pool.indirect_dma_start(hflat[:, (2 * (t % 2) + c) * D:(2 * (t % 2) + c + 1) * D], None, y_dram[:, :],
                                            bass.IndirectOffsetOnAxis(ap=rowi[:, c, t:t + 1], axis=0)).then_inc(fin_in[t % 2], 16)

        block = ctx.enter_context(nc.Block())

        @block.sync
        def _(sp):
            for t in range(TT):
                sp.dma_start(x[:, t, :], x_in[t * P:(t + 1) * P, :]).then_inc(x_in_s[t], 16)
            for L in range(DEPTH):
                if L:
                    sp.wait_ge(tile_used, FT + 7)
                sp.dma_start(q_w, w_q[L]).then_inc(wq_in, 16)
                sp.dma_start(kv_w, w_kv[L]).then_inc(wkv_in, 16)
                if L:
                    sp.wait_ge(tile_used, FT + 8)
                sp.dma_start(kc_w, w_kc[L]).then_inc(wkc_in, 16)
                for c in range(CT):
                    sp.dma_start(cv_w[c], w_cv[L, c]).then_inc(wcv_in[c], 16)
                if L == 0:
                    sp.wait_ge(bias_out, 16)
                sp.wait_ge(pq_done, TT * (L + 1))
                sp.dma_start(T, shifted_dram.ap().rearrange("h p n -> p h n")).then_inc(T_in, 16)
                sp.wait_ge(pkv_done, TT * (L + 1))
                sp.dma_start(W1, w_1[L]).then_inc(w1_in, 16)
                sp.wait_ge(pcv_done, CT * (L + 1))
                sp.dma_start(WO, w_o[L]).then_inc(wo_in, 16)
                if L == 0:
                    for i in range(FT):
                        s = i % NSLOT
                        if i == 1:
                            sp.wait_ge(po_ps, TT * (L + 1))
                        if i >= NSLOT:
                            sp.wait_ge(tile_used, i - NSLOT + 1)
                        sp.dma_start(slot[s][:, 0:2 * KD * P], f_gu[i]).then_inc(slot_in[s], 16)
                    for s in range(NSLOT):
                        sp.wait_ge(tile_used, NSLOT + s + 1)
                        sp.dma_start(slot[s][:, 0:2 * KD * P], f_dn[s]).then_inc(slot_in[s], 16)
                else:
                    moe_loads(sp)

        @block.tensor
        def _(pe):
            pe.wait_ge(const_in, 16)
            def norm_transposes(ns):
                for t in range(TT):
                    pe.wait_ge(xn_done, 4 * ns + t + 1)
                    for hf in range(2):
                        i = 2 * t + hf
                        if i >= 4:
                            pe.wait_ge(htd if hf else hta, 4 * ns + t - 1)
                        for k in range(4):
                            m = tr(ps[:, 4 + i % 4, k * P:(k + 1) * P], xn[:, t % 2, (4 * hf + k) * P:(4 * hf + k + 1) * P], ident)
                        m.then_inc(xt_done, 1)

            def layer(L):
                norm_transposes(2 * L)

                def natural(bank, t, w, n, done, col=0):
                    for k in range(KD):
                        m = mm(ps[:, bank, col:col + n], hT[:, k, t * P:(t + 1) * P], w[:, k, :], start=(k == 0), stop=(k == KD - 1))
                    if done is not None:
                        m.then_inc(done, 1)

                def channels(bank, w, col, done):
                    for k in range(KD):
                        m = mm(ps[:, bank, :], w[:, k, col:col + P], hT[:, k, :], start=(k == 0), stop=(k == KD - 1))
                    if done is not None:
                        m.then_inc(done, 1)

                pe.wait_ge(wq_in, 16 * (L + 1))
                for t in range(TT):
                    pe.wait_ge(hta, 8 * L + t + 1)
                    pe.wait_ge(htd, 8 * L + t + 1)
                    natural(t, t, q_w, 512, pq_done)
                pe.wait_ge(wkv_in, 16 * (L + 1))
                for t in range(TT):
                    natural(4 + t, t, kv_w, 512, pkv_done)
                    pe.wait_ge(qn_done, TT * L + t + 1)
                    for i in range(4):
                        m = tr(ps[:, t, i * P:(i + 1) * P], qn[:, i * P:(i + 1) * P], ident)
                    m.then_inc(qt_ps, 1)

                def kt(t):
                    pe.wait_ge(kn_done, TT * L + t + 1)
                    pe.wait_ge(v_done, TT * L + t + 1)
                    for i in range(4):
                        m = tr(ps[:, 4 + t, i * P:(i + 1) * P], kn[:, i * P:(i + 1) * P], ident)
                    m.then_inc(kt_ps, 1)

                pe.wait_ge(wkc_in, 16 * (L + 1))
                for a in range(2):
                    pe.wait_ge(qt_done, TT * L + a + 1)
                    channels(a, kc_w, a * P, pkc_done)
                    kt(a)
                pe.wait_ge(qt_done, TT * L + 3)
                for t in range(TT):
                    natural(2, t, kc_w[:, :, 2 * P:KCW], 24, pkc_done if t == TT - 1 else None, col=24 * t)
                kt(2)
                kt(3)

                def conv(c):
                    pe.wait_ge(wcv_in[c], 16 * (L + 1))
                    if c == 0:
                        pe.wait_ge(kt_done, TT * L + 3)
                    elif c == 1:
                        pe.wait_ge(z_done, 2 * L + 2)
                        pe.wait_ge(gexp_done, L + 1)
                    else:
                        pe.wait_ge(cv_done, CT * L + c - 1)
                    b0 = 0 if c % 2 else 4
                    for j in range(3):
                        channels(b0 + j, cv_w[c], j * P, pcv_done if j == 2 else None)

                if L == 0:
                    pe.wait_ge(table_in, 32)
                    pe.wait_ge(zeroed, 1)
                    pe.wait_ge(qt_done, TT)
                    pe.wait_ge(kt_done, TT)
                    for i in range(2):
                        m = mm(ps[0:H, 3 + 4 * i, 0:320], table_sb[0:33, :], oh_sb[0:33, i * 320:(i + 1) * 320], start=True, stop=True)
                    m.then_inc(bias_ps, 1)
                conv(0)
                conv(1)
                if L == 0:
                    pe.wait_ge(bias_sb, 1)
                pe.wait_ge(w1_in, 16 * (L + 1))
                pe.wait_ge(qt_done, TT * L + 4)
                for a in range(2):
                    for l in range(LP):
                        mm(ps[:, 3, a * P:a * P + 2 * NCMP].rearrange("p (g n) -> p g n", g=G), W1[:, a, l, :],
                           Z[:, a, :, l:l + 8 * NCMP - 7:8], start=(l == 0), stop=(l == LP - 1))
                    for l in range(LP):
                        m = mm(ps[:, 3, a * P + 100:a * P + 101], W1[:, a, l, :],
                               pc[:, PC_POS + a * LP + l:PC_POS + a * LP + l + 1], start=(l == 0), stop=(l == LP - 1))
                m.then_inc(hp_done, 1)
                conv(2)
                pe.wait_ge(gelu_done, L + 1)
                pe.wait_ge(kt_done, TT * L + 4)
                for a in range(2):
                    for g in range(G):
                        m = mm(ps[0:NCMP, 7, (2 * a + g) * DH:(2 * a + g + 1) * DH], hidc[:, a, g * NCMP:(g + 1) * NCMP],
                               pc[:, PC_W2 + a * DH:PC_W2 + (a + 1) * DH], start=True, stop=True)
                m.then_inc(ho_done, 1)
                conv(3)
                pe.wait_ge(kcn_done, L + 1)
                pe.wait_ge(vbd_done, L + 1)
                for g in range(G):
                    m = tr(ps[:, 7, 256 + 32 * g:256 + 32 * g + NCMP], kn[0:NCMP, g * P:(g + 1) * P], ident[0:NCMP, 0:NCMP])
                m.then_inc(kct_ps, 1)
                pe.wait_ge(sqs_done, CT * (L + 1))
                for t in range(TT):
                    m = mm(ps[:, 3, t:t + 1], sqsum[:, t * P:(t + 1) * P], ones[:, 0:1], start=True, stop=True)
                m.then_inc(cs_ps, 1)

                def scores(u):
                    t, h, b = u // 16, (u % 16) // 2, u % 2
                    p0, n = DH * (h % 2), P * (t + 1)
                    if u < 2:
                        pe.wait_ge(cv_done, CT * (L + 1))
                    if u >= 2:
                        pe.wait_ge(sb_done, 64 * L + u - 1)
                    mm(ps[:, u % 2, 0:n], qT[p0:p0 + DH, h // 2, t * P:(t + 1) * P], kT[p0:p0 + DH, 2 * b + h // R, 0:n],
                       start=True, stop=True).then_inc(s_ps, 1)

                def turn(u):
                    t = u // 16
                    pe.wait_ge(p_done, 64 * L + u + 1)
                    if u == 1:
                        pe.wait_ge(rc_done, L + 1)
                    if u >= 2:
                        pe.wait_ge(pta if u % 2 else ptd, 32 * L + u // 2)
                    for i in range(t + 1):
                        m = tr(ps[:, 2 + u % 2, i * P:(i + 1) * P], sb_p[:, u % 2, i * P:(i + 1) * P], ident)
                    m.then_inc(pt_ps, 1)

                def values(u):
                    t, h, b = u // 16, (u % 16) // 2, u % 2
                    pe.wait_ge(ptd if b == 0 else pta, 32 * L + u // 2 + 1)
                    if u % 16 == 0 and t:
                        pe.wait_ge(o_read, TT * L + t)
                    for i in range(t + 1):
                        m = mm(ps[:, 4 + b, h * DH:(h + 1) * DH], sb_pt[:, u % 2, i * P:(i + 1) * P],
                               V[:, i, b * P + (h // R) * DH:b * P + (h // R + 1) * DH], start=(i == 0), stop=(i == t))
                    m.then_inc(o_ps, 1)

                def cmp_scores(t):
                    n = KD * t + 7
                    pe.wait_ge(kct_done, L + 1)
                    if t:
                        pe.wait_ge(cpt_done, TT * L + t)
                        pe.wait_ge(ot_done, TT * L + t)
                    for h in range(H):
                        p0 = DH * (h % 2)
                        m = mm(ps[:, 6 + h % 2, 32 * (h // 2):32 * (h // 2) + n], qT[p0:p0 + DH, h // 2, t * P:(t + 1) * P],
                               kcT[p0:p0 + DH, h // R, 0:n], start=True, stop=True)
                    m.then_inc(cs1_ps, 1)

                def cmp_turn(t):
                    pe.wait_ge(cp_done, TT * L + t + 1)
                    for g in range(G):
                        m = tr(ps[:, 6, 256 + g * P:256 + (g + 1) * P], Pc[:, g * R:(g + 1) * R, :].rearrange("p r n -> p (r n)"), ident)
                    m.then_inc(cpt_ps, 1)

                def cmp_values(t):
                    pe.wait_ge(cpt_done, TT * L + t + 1)
                    for g in range(G):
                        m = mm(ps[:, 7, g * 256:(g + 1) * 256], PcT[:, g, :], vbd[:, g, :], start=True, stop=True)
                    m.then_inc(co_ps, 1)

                def o_turn(t):
                    pe.wait_ge(og_done, TT * L + t + 1)
                    for i in range(4):
                        m = tr(ps[:, 7, i * P:(i + 1) * P], on[:, i * P:(i + 1) * P], ident)
                    m.then_inc(ot_ps, 1)

                pe.wait_ge(T_in, 16 * (L + 1))
                for i in range(64 + 3):
                    t, r = i // 16, i % 16
                    if 2 <= i < 66:
                        turn(i - 2)
                    if i < 64:
                        scores(i)
                    if i >= 3:
                        values(i - 3)
                    if r == 5 and t:
                        o_turn(t - 1)
                    if r == 6:
                        cmp_scores(t)
                    if r == 8:
                        cmp_turn(t)
                    if r == 10:
                        cmp_values(t)
                o_turn(TT - 1)

                pe.wait_ge(wo_in, 16 * (L + 1))
                for t in range(TT):
                    pe.wait_ge(ot_done, TT * L + t + 1)
                    if t == 0:
                        pe.wait_ge(cvm_done, CT * (L + 1))
                    b0 = 4 * (t % 2)
                    if t == 1:
                        pe.wait_ge(ot_done, TT * (L + 1))
                    if t >= 2:
                        pe.wait_ge(xres, TT * L + t - 1)
                    for j in range(4):
                        part, hf = j // 2, j % 2
                        for k in range(4):
                            m = mm(ps[:, b0 + j, :], mixT[:, 4 * part + k, t * P:(t + 1) * P],
                                   WO[:, 4 * part + k, hf * 512:(hf + 1) * 512], start=(k == 0), stop=(k == 3))
                    m.then_inc(po_ps, 1)
                norm_transposes(2 * L + 1)
                pe.wait_ge(hta, 8 * L + 8)
                pe.wait_ge(htd, 8 * L + 8)

            def ffn():
                for i in range(FT):
                    s = i % NSLOT
                    pe.wait_ge(slot_in[s], 16 * (i // NSLOT + 1))
                    if i >= 2:
                        pe.wait_ge(fh_done, i - 1)
                    for j, w in enumerate((gate_w[s], up_w[s])):
                        for k in range(KD):
                            m = mm(ps[:, 2 * (i % 2) + j, :], w[:, k, :], hT[:, k, :], start=(k == 0), stop=(k == KD - 1))
                        m.then_inc(tile_used if j else fg_ps, 1)
                pe.wait_ge(fh_done, FT)
                for s in range(NSLOT):
                    pe.wait_ge(slot_in[s], 48)
                    for i in range(2):
                        for t in range(TT):
                            for hf in range(2):
                                first, last = (s == 0 and i == 0), (s == NSLOT - 1 and i == 1)
                                m = mm(ps[:, 2 * t + hf, :], down_w[s][:, i * 512 + t * P:i * 512 + (t + 1) * P],
                                       slot[s][:, i * D + hf * 512:i * D + (hf + 1) * 512], start=first, stop=last)
                                if last and not (t == TT - 1 and hf == 1):
                                    m.then_inc(fd_ps, 1)
                    m.then_inc(tile_used, 1)

            layer(0)
            ffn()
            layer(1)
            moe_products(pe)

        @block.vector
        def _(dve):
            chain = [0]

            def after(ins):
                chain[0] += 1
                ins.then_inc(dch, 1)
                dve.wait_ge(dch, chain[0])

            powers = [0]

            def rsqrt(dst, src, n, post=1.0):
                powers[0] += 1
                v.tensor_scalar(dst, src, 1.0 / (n * post ** 2), EPS / post ** 2, ALU.mult, ALU.add).then_inc(power_in, 1)
                dve.wait_ge(power_out, powers[0])

            v.memset(table_sb[32:33, :], NEG).then_inc(zeroed, 1)
            v.memset(zc[:, 0:2], 0.0)
            v.memset(vbd[:, :, :], 0.0)
            dve.wait_ge(const_in, 16)

            def norm(ns):
                dve.wait_ge(gain_in, 16 * (ns + 1))
                for t in range(TT):
                    dve.wait_ge(ss_done, 4 * ns + t + 1)
                    rsqrt(rstd[:, t:t + 1], ss[:, t:t + 1], D)
                    if 8 * ns + 2 * t - 2 > 0:
                        dve.wait_ge(xt_done, 8 * ns + 2 * t - 2)
                    if ns == 3 and t >= 2:
                        dve.wait_ge(h_out[t % 2], 16)
                    v.scalar_tensor_tensor(xn[:, t % 2, :], x[:, t, :], rstd[:, t:t + 1], gb[:, :], ALU.mult, ALU.mult).then_inc(xn_done, 1)
                    if t >= 1:
                        norm_copy(ns, t - 1)
                norm_copy(ns, TT - 1)

            def norm_copy(ns, t):
                dve.wait_ge(xt_done, 8 * ns + 2 * t + 2)
                v.tensor_copy(hT[:, 4:8, t * P:(t + 1) * P], ps[:, 4 + (2 * t + 1) % 4, :].rearrange("p (k n) -> p k n", k=4)).then_inc(htd, 1)

            def reduce_heads(L, i, n=P):
                dve.wait_ge(sq_done, 9 * L + i + 1)
                g = H if n == P else G
                v.tensor_reduce(ssh[0:n, 0:g], sqb[0:n, 0:g * DH].rearrange("p (h n) -> p h n", h=g), AX, ALU.add).then_inc(red_done, 1)
                dve.wait_ge(red_done, 9 * L + i + 1)

            def layer(L):
                norm(2 * L)
                dve.wait_ge(params_in, 32 * (L + 1))
                kn_g = pb[:, B_KN:B_END].rearrange("p (b n) -> p b n", b=3)
                after(v.tensor_tensor(kn_g, kn_g, bc_mid(pb[:, B_QN:B_KN], 1, 3), ALU.mult))
                for t in range(TT):
                    reduce_heads(L, t)
                    rsqrt(rh, ssh, DH, DH ** -0.5)
                    if TT * L + t:
                        dve.wait_ge(qt_ps, TT * L + t)
                    if L and t == 0:
                        dve.wait_ge(spare_rows, 16 * (-(-(MAXR - E) * CAP // P) - 2))
                        dve.wait_ge(y_out, 32)
                    v.tensor_tensor(qn[:, :].rearrange("p (h n) -> p h n", h=H), ps[:, t, :].rearrange("p (h n) -> p h n", h=H),
                                    bc_last(rh, DH), ALU.mult).then_inc(qn_done, 1)
                for t in range(TT):
                    reduce_heads(L, TT + t)
                    rsqrt(rh, ssh, DH)
                    if t:
                        dve.wait_ge(kt_ps, TT * L + t)
                    kk = kn[:, :].rearrange("p (b g u n) -> p b g u n", b=2, g=G, u=2)
                    dve.wait_ge(v_done, TT * L + t + 1)
                    src = ps[:, 4 + t, :].rearrange("p (b u n) -> p b u n", b=2, u=2)[:, :, 0, :].rearrange("p b (g n) -> p b g n", g=G)
                    r4 = rh.rearrange("p (b u g) -> p b u g", b=2, u=2)[:, :, 0, :]
                    after(v.tensor_tensor(yc[:, 0:256].rearrange("p (b g n) -> p b g n", b=2, g=G), src, bc_last(r4, DH), ALU.mult))
                    for u in range(2):
                        m = v.tensor_tensor(kk[:, :, :, u, :], yc[:, 0:256].rearrange("p (b g n) -> p b g n", b=2, g=G),
                                            bc_mid(kn_g[:, 1:3, :], 2, G), ALU.mult)
                    m.then_inc(kn_done, 1)
                if L == 0:
                    dve.wait_ge(bias_ps, 1)
                    for i in range(2):
                        m = v.tensor_copy(bias_row[:, 320 * i:320 * (i + 1)], ps[0:H, 3 + 4 * i, 0:320])
                    m.then_inc(bias_sb, 1)
                dve.wait_ge(gexp_done, L + 1)
                gf = gts[:, :, :, :].rearrange("p t h b -> p (t h b)")
                after(v.tensor_scalar(gf, gf, 1.0, None, ALU.add))
                v.reciprocal(gf, gf).then_inc(gate_done, 1)

                def conv(c):
                    w = lambda j: pc[:, PC_CONV + 3 * c + j:PC_CONV + 3 * c + j + 1]
                    b0 = 0 if c % 2 else 4
                    dve.wait_ge(cc_done, CT * L + c + 1)
                    after(v.tensor_tensor(zc[:, 2:S + 2], ccb[:, :], ps[:, b0 + 2, :], ALU.mult))
                    if CT * L + c:
                        dve.wait_ge(cvm_done, CT * L + c)
                    after(v.tensor_scalar(yc[:, :], zc[:, 2:S + 2], w(2), None, ALU.mult))
                    after(v.scalar_tensor_tensor(yc[:, :], zc[:, 1:S + 1], w(1), yc[:, :], ALU.mult, ALU.add))
                    after(v.scalar_tensor_tensor(yc[:, :], zc[:, 0:S], w(0), yc[:, :], ALU.mult, ALU.add))
                    v.tensor_tensor(yc[:, :], yc[:, :], ps[:, b0, :], ALU.mult).then_inc(cv_done, 1)
                    dve.wait_ge(cvm_done, CT * L + c + 1)
                    if c == 0:
                        if L:
                            dve.wait_ge(cs_ps, L)
                        v.tensor_copy(sqsum[:, :], ccb[:, :]).then_inc(sqs_done, 1)
                    else:
                        dve.wait_ge(sqs_done, CT * L + c)
                        v.tensor_tensor(sqsum[:, :], sqsum[:, :], ccb[:, :], ALU.add).then_inc(sqs_done, 1)

                conv(0)
                conv(1)
                dve.wait_ge(hp_done, L + 1)
                v.tensor_copy(posb, ps[:, 3, 100:100 + P + 1:P]).then_inc(pos_done, 1)
                conv(2)
                reduce_heads(L, 8, NCMP)
                rsqrt(rh[0:NCMP, 0:G], ssh[0:NCMP, 0:G], DH)
                dve.wait_ge(kt_ps, TT * (L + 1))
                src = ps[0:NCMP, 7, 0:2 * DH].rearrange("p (g n) -> p g n", g=G)
                tmp = qn[0:NCMP, 0:2 * DH].rearrange("p (g n) -> p g n", g=G)
                dve.wait_ge(qt_ps, TT * (L + 1))
                after(v.tensor_tensor(tmp, src, bc_last(rh[0:NCMP, 0:G], DH), ALU.mult))
                kk = kn[0:NCMP, 0:4 * DH].rearrange("p (g u n) -> p g u n", g=G, u=2)
                for u in range(2):
                    m = v.tensor_tensor(kk[:, :, u, :], tmp, bc_mid(kn_g[0:NCMP, 0, :], 1, G), ALU.mult)
                m.then_inc(kcn_done, 1)
                if L:
                    dve.wait_ge(co_ps, TT * L)
                for g in range(G):
                    for r in range(R):
                        m = v.tensor_copy(vbd[32 * r:32 * r + NCMP, g, r * DH:(r + 1) * DH], ps[0:NCMP, 7, (2 + g) * DH:(3 + g) * DH])
                m.then_inc(vbd_done, 1)
                conv(3)
                dve.wait_ge(cs_ps, L + 1)
                rsqrt(rc, ps[:, 3, 0:TT], CW)
                v.memset(Pc[:, :, :], 0.0).then_inc(rc_done, 1)

                dve.wait_ge(T_in, 16 * (L + 1))

                def scores(u):
                    t, h = u // 16, (u % 16) // 2
                    n = P * (t + 1)
                    dve.wait_ge(s_ps, 64 * L + u + 1)
                    if u >= 2:
                        dve.wait_ge(p_done, 64 * L + u - 1)
                    v.tensor_tensor_reduce(sb_s[:, u % 2, 0:n], ps[:, u % 2, 0:n], T[:, h, 384 - P * t:384 - P * t + n],
                                           -1.0, 3e38, ALU.add, ALU.min, negm[:, u % 16:u % 16 + 1]).then_inc(sb_done, 1)

                def pt_copy(u):
                    n = P * (u // 16 + 1)
                    dve.wait_ge(pt_ps, 64 * L + u + 1)
                    if u >= 2:
                        dve.wait_ge(o_ps, 64 * L + u - 1)
                    v.tensor_copy(sb_pt[:, u % 2, 0:n], ps[:, 2 + u % 2, 0:n]).then_inc(ptd, 1)

                def cmp_scores(t):
                    n = KD * t + 7
                    dve.wait_ge(cs1_ps, TT * L + t + 1)
                    if TT * L + t:
                        dve.wait_ge(cp_done, TT * L + t)
                    y0 = 415 - P * t
                    halves = lambda ap: ap.rearrange("p (j a) n -> p a j n", a=2)
                    after(v.tensor_tensor(halves(Sc[:, :, 0:n]), ps[:, 6:8, 0:P].rearrange("p a (j n) -> p a j n", n=32)[:, :, :, 0:n],
                                          halves(T[:, :, y0:y0 + 16 * n - 15:16]), ALU.add))
                    after(v.tensor_reduce(cmx, Sc[:, :, 0:n], AX, ALU.max))
                    v.tensor_tensor(Sc[:, :, 0:n], Sc[:, :, 0:n], bc_last(cmx, n), ALU.subtract).then_inc(csub_done, 1)

                def cmp_sum(t):
                    n = KD * t + 7
                    dve.wait_ge(cp_done, TT * L + t + 1)
                    after(v.tensor_reduce(den[t % 2][:, 0, :], Pc[:, :, 0:n], AX, ALU.add))

                def combine(t):
                    dve.wait_ge(p_done, 64 * L + 16 * t + 16)
                    dve.wait_ge(gate_done, L + 1)
                    dflat = st[:, 40 + 64 * (t % 2):64 + 64 * (t % 2)]
                    after(v.tensor_scalar(dflat, dflat, 1e-30, None, ALU.max))
                    after(v.reciprocal(dflat, dflat))
                    after(v.tensor_tensor(coef, den[t % 2], gts[:, t, :, :].rearrange("p h b -> p b h"), ALU.mult))
                    if t == 0:
                        after(v.tensor_scalar(coef[:, 0, :], coef[:, 0, :], cst[:, C_VALID:C_VALID + 1], None, ALU.mult))
                    o3 = on[:, :].rearrange("p (h n) -> p h n", h=H)
                    t3 = on_t[:, :].rearrange("p (h n) -> p h n", h=H)
                    bank = lambda b: ps[:, b, :].rearrange("p (h n) -> p h n", h=H)
                    dve.wait_ge(co_ps, TT * L + t + 1)
                    if TT * L + t:
                        dve.wait_ge(ot_ps, TT * L + t)
                    dve.wait_ge(kct_ps, L + 1)
                    dve.wait_ge(o_ps, 64 * L + 16 * t + 16)
                    after(v.tensor_tensor(o3, bank(4), bc_last(coef[:, 1, :], DH), ALU.mult))
                    v.tensor_tensor(t3, bank(5), bc_last(coef[:, 2, :], DH), ALU.mult).then_inc(o_read, 1)
                    dve.wait_ge(o_read, TT * L + t + 1)
                    after(v.tensor_tensor(o3, o3, t3, ALU.add))
                    after(v.tensor_tensor(t3, bank(7), bc_last(coef[:, 0, :], DH), ALU.mult))
                    v.tensor_tensor(o3, o3, t3, ALU.add).then_inc(comb_done, 1)

                def gain(t):
                    dve.wait_ge(ssa_done, TT * L + t + 1)
                    v.tensor_tensor(on[:, :], on[:, :], pb[:, B_AN:B_QN], ALU.mult).then_inc(og_done, 1)

                for i in range(64 + 3):
                    t, r = i // 16, i % 16
                    if 2 <= i < 66 and i % 2 == 0:
                        pt_copy(i - 2)
                    if i < 64:
                        scores(i)
                    if r == 3 and t:
                        gain(t - 1)
                    if r == 2 and t:
                        combine(t - 1)
                    if r == 6:
                        cmp_scores(t)
                    if r == 8:
                        cmp_sum(t)
                gain(TT - 1)
                rsqrt(ra, ssa, 512)
                for t in range(TT):
                    dve.wait_ge(po_ps, TT * L + t + 1)
                    for j in range(4):
                        xs = x[:, t, (j % 2) * 512:(j % 2 + 1) * 512]
                        r = (ra if j < 2 else rc)[:, t:t + 1]
                        m = v.scalar_tensor_tensor(xs, ps[:, 4 * (t % 2) + j, :], r, xs, ALU.mult, ALU.add)
                        if j == 1:
                            after(m)
                    m.then_inc(xres, 1)
                norm(2 * L + 1)

            def ffn():
                v.memset(qk[:, :, :], 0.0).then_inc(zeroed, 1)
                for i in range(FT):
                    dve.wait_ge(tile_used, i + 1)
                    dve.wait_ge(fsg_done, i + 1)
                    v.tensor_tensor(down_w[i % NSLOT][:, (i // NSLOT) * 512:(i // NSLOT + 1) * 512], sb_s[:, i % 2, :],
                                    ps[:, 2 * (i % 2) + 1, :], ALU.mult).then_inc(fh_done, 1)
                dve.wait_ge(tile_used, FT + NSLOT)
                for t in range(TT):
                    for hf in range(2):
                        xs = x[:, t, hf * 512:(hf + 1) * 512]
                        m = v.tensor_tensor(xs, xs, ps[:, 2 * t + hf, :], ALU.add)
                    m.then_inc(xffn, 1)

            layer(0)
            ffn()
            layer(1)
            moe_vector(dve, after)

        @block.scalar
        def _(se):
            def norm(ns):
                for t in range(TT):
                    if ns == 0:
                        se.wait_ge(x_in_s[t], 16)
                    elif ns == 2:
                        se.wait_ge(xffn, t + 1)
                    else:
                        se.wait_ge(xres, TT * (ns // 2) + t + 1)
                    if ns or t:
                        se.wait_ge(ss_done, 4 * ns + t)
                    act(junk, x[:, t, :], ACT.Square, accum_out=ss[:, t:t + 1]).then_inc(ss_done, 1)
                    if t >= 1:
                        norm_copy(ns, t - 1)
                norm_copy(ns, TT - 1)

            def norm_copy(ns, t):
                se.wait_ge(xt_done, 8 * ns + 2 * t + 1)
                nc.scalar.copy(hT[:, 0:4, t * P:(t + 1) * P], ps[:, 4 + (2 * t) % 4, :].rearrange("p (k n) -> p k n", k=4)).then_inc(hta, 1)

            def square(L, i, src, n=P, w=512):
                if 9 * L + i:
                    se.wait_ge(red_done, 9 * L + i)
                act(sqb[0:n, 0:w], src, ACT.Square).then_inc(sq_done, 1)

            def layer(L):
                norm(2 * L)
                for t in range(TT):
                    se.wait_ge(pq_done, TT * L + t + 1)
                    square(L, t, ps[:, t, :])
                for t in range(TT):
                    se.wait_ge(pkv_done, TT * L + t + 1)
                    square(L, TT + t, ps[:, 4 + t, :])
                    nc.scalar.copy(V[:, t, :].rearrange("p (b n) -> p b n", b=2),
                                   ps[:, 4 + t, :].rearrange("p (b u n) -> p b u n", b=2, u=2)[:, :, 1, :]).then_inc(v_done, 1)
                    se.wait_ge(qt_ps, TT * L + t + 1)
                    nc.scalar.copy(qT[:, :, t * P:(t + 1) * P], ps[:, t, :].rearrange("p (k n) -> p k n", k=4)).then_inc(qt_done, 1)

                def kt(t):
                    se.wait_ge(kt_ps, TT * L + t + 1)
                    nc.scalar.copy(kT[:, :, t * P:(t + 1) * P], ps[:, 4 + t, :].rearrange("p (k n) -> p k n", k=4)).then_inc(kt_done, 1)

                for a in range(2):
                    se.wait_ge(pkc_done, 3 * L + a + 1)
                    for g in range(G):
                        for odd in range(2):
                            m = nc.scalar.copy(Z[odd * DH:(odd + 1) * DH, a, g, :], ps[g * DH:(g + 1) * DH, a, odd:S:2])
                    m.then_inc(z_done, 1)
                    kt(a)
                se.wait_ge(pkc_done, 3 * L + 3)
                if L:
                    se.wait_ge(comb_done, TT * L)
                act(gts[:, :, :, :].rearrange("p t h b -> p (t h b)"), ps[:, 2, 0:96], ACT.Exp, scale=-1.0).then_inc(gexp_done, 1)
                kt(2)
                kt(3)

                def conv(c):
                    b0 = 0 if c % 2 else 4
                    se.wait_ge(pcv_done, CT * L + c + 1)
                    if CT * L + c:
                        se.wait_ge(sqs_done, CT * L + c)
                    nc.scalar.copy(ccb[:, :], ps[:, b0 + 1, :]).then_inc(cc_done, 1)
                    se.wait_ge(cv_done, CT * L + c + 1)
                    act(mixT[:, 4 + c, :], yc[:, :], ACT.Copy, scale=pc[:, PC_CN + c:PC_CN + c + 1])
                    act(ccb[:, :], yc[:, :], ACT.Square).then_inc(cvm_done, 1)

                se.wait_ge(params_in, 32 * (L + 1))
                if L == 0:
                    se.wait_ge(bias_stored, 16)
                conv(0)
                conv(1)
                se.wait_ge(pos_done, L + 1)
                for a in range(2):
                    m = act(hidc[:, a, :], ps[:, 3, a * P:a * P + 2 * NCMP], ACT.Gelu_apprx_tanh, bias=posb[:, a:a + 1])
                m.then_inc(gelu_done, 1)
                conv(2)
                se.wait_ge(ho_done, L + 1)
                square(L, 8, ps[0:NCMP, 7, 0:2 * DH], NCMP, 2 * DH)
                conv(3)
                se.wait_ge(kct_ps, L + 1)
                nc.scalar.copy(kcT[:, :, 0:NCMP], ps[:, 7, 256:320].rearrange("p (g n) -> p g n", g=G)[:, :, 0:NCMP]).then_inc(kct_done, 1)

                def probs(u):
                    t, h, b = u // 16, (u % 16) // 2, u % 2
                    n = P * (t + 1)
                    se.wait_ge(sb_done, 64 * L + u + 1)
                    if u >= 2:
                        se.wait_ge(pt_ps, 64 * L + u - 1)
                    if u % 16 == 0 and TT * L + t > 1:
                        se.wait_ge(comb_done, TT * L + t - 1)
                    if u == 0:
                        se.wait_ge(sqs_done, CT * (L + 1))
                    act(sb_p[:, u % 2, 0:n], sb_s[:, u % 2, 0:n], ACT.Exp, bias=negm[:, u % 16:u % 16 + 1], scale=-1.0,
                        accum_out=den[t % 2][:, 1 + b, h:h + 1]).then_inc(p_done, 1)

                def pt_copy(u):
                    n = P * (u // 16 + 1)
                    se.wait_ge(pt_ps, 64 * L + u + 1)
                    if u >= 2:
                        se.wait_ge(o_ps, 64 * L + u - 1)
                    nc.scalar.copy(sb_pt[:, u % 2, 0:n], ps[:, 2 + u % 2, 0:n]).then_inc(pta, 1)

                def cmp_probs(t):
                    n = KD * t + 7
                    se.wait_ge(csub_done, TT * L + t + 1)
                    if TT * L + t:
                        se.wait_ge(cpt_ps, TT * L + t)
                    act(Pc[:, :, 0:n], Sc[:, :, 0:n], ACT.Exp).then_inc(cp_done, 1)

                def cmp_pt(t):
                    se.wait_ge(cpt_ps, TT * L + t + 1)
                    if TT * L + t:
                        se.wait_ge(co_ps, TT * L + t)
                    nc.scalar.copy(PcT[:, :, :], ps[:, 6, 256:512].rearrange("p (g n) -> p g n", g=G)).then_inc(cpt_done, 1)

                def attn_norm(t):
                    se.wait_ge(comb_done, TT * L + t + 1)
                    act(ccb[:, :], on[:, :], ACT.Square, accum_out=ssa[:, t:t + 1]).then_inc(ssa_done, 1)

                def o_copy(t):
                    se.wait_ge(ot_ps, TT * L + t + 1)
                    nc.scalar.copy(mixT[:, 0:4, t * P:(t + 1) * P], ps[:, 7, :].rearrange("p (k n) -> p k n", k=4)).then_inc(ot_done, 1)

                for i in range(64 + 3):
                    t, r = i // 16, i % 16
                    if 2 <= i < 66 and i % 2:
                        pt_copy(i - 2)
                    if i < 64:
                        probs(i)
                    if r == 2 and t:
                        attn_norm(t - 1)
                    if r == 5 and t:
                        o_copy(t - 1)
                    if r == 7:
                        cmp_probs(t)
                    if r == 8:
                        cmp_pt(t)
                o_copy(TT - 1)
                norm(2 * L + 1)

            def ffn():
                se.wait_ge(zeroed, 2)
                for i in range(E * CAP, MAXR * CAP, P):
                    n = min(P, MAXR * CAP - i)
                    done = y_out if i >= MAXR * CAP - 2 * P else spare_rows
                    se.dma_start(y_dram[i:i + n, :], qk[0:n, :, :].rearrange("p a n -> p (a n)")).then_inc(done, 16)
                for i in range(FT):
                    se.wait_ge(fg_ps, i + 1)
                    if i >= 2:
                        se.wait_ge(fh_done, i - 1)
                    act(sb_s[:, i % 2, :], ps[:, 2 * (i % 2), :], ACT.Silu).then_inc(fsg_done, 1)

            layer(0)
            ffn()
            layer(1)
            moe_scalar(se)

        @block.gpsimd
        def _(pool):
            pool.dma_start(gb[:, :], n_b[0:1, :].to_broadcast([P, D])).then_inc(gain_in, 16)
            pool.dma_start(cst[:, :], const).then_inc(const_in, 16)
            pool.dma_start(pb[:, :], p_b[0:1, :].to_broadcast([P, B_END])).then_inc(params_in, 16)
            pool.dma_start(pc[:, :], p_c[0]).then_inc(params_in, 16)
            pool.dma_start(table_sb[0:32, :], table).then_inc(table_in, 16)
            pool.dma_start(oh_sb[0:33, :], onehot).then_inc(table_in, 16)
            pool.wait_ge(const_in, 16)
            taken = [0]

            def power(*aps):
                for ap in aps:
                    taken[0] += 1
                    pool.wait_ge(power_in, taken[0])
                    n = ap.shape[0]
                    nc.gpsimd.tensor_tensor(ap, ap, cst[0:n, C_EXP:C_EXP + ap.shape[1]], ALU.pow).then_inc(power_out, 1)

            for L in range(DEPTH):
                power(*(rstd[:, t:t + 1] for t in range(TT)))
                pool.wait_ge(xn_done, 8 * L + 4)
                pool.dma_start(gb[:, :], n_b[2 * L + 1:2 * L + 2, :].to_broadcast([P, D])).then_inc(gain_in, 16)
                power(*([rh] * (2 * TT)))
                if L == 0:
                    pool.wait_ge(bias_sb, 1)
                    pool.dma_start(bias_dram.ap(), bias_row[:, :]).then_inc(bias_stored, 16)
                    pool.wait_ge(bias_stored, 16)
                    pool.dma_start(shifted_dram.ap(), bass.AP(bias_dram, P - 1, [[ZLEN, H], [-1, P], [1, S]])).then_inc(bias_out, 16)
                power(rh[0:NCMP, 0:G], rc, ra)
                if L == 0:
                    pool.wait_ge(ho_done, 1)
                    pool.dma_start(pb[:, :], p_b[1:2, :].to_broadcast([P, B_END])).then_inc(params_in, 16)
                    pool.dma_start(pc[:, :], p_c[1]).then_inc(params_in, 16)
                power(*(rstd[:, t:t + 1] for t in range(TT)))
                if L == 0:
                    pool.wait_ge(xn_done, 8)
                    pool.dma_start(gb[:, :], n_b[2:3, :].to_broadcast([P, D])).then_inc(gain_in, 16)
            moe_gathers(pool)


def shape_constants():
    c = np.zeros((P, C_END), np.float32)
    p = np.arange(P)
    c[:, C_ID:C_ID + P] = np.eye(P)
    c[:, C_ONE:C_ONE + P] = 1
    c[:, C_TRI:C_TRI + P] = p[:, None] < p[None, :]
    c[:, C_IOTA:C_IOTA + CAP] = np.arange(CAP)
    c[:, C_TOK:C_TOK + TT] = p[:, None] + P * np.arange(TT)
    c[:, C_I8:C_I8 + E] = np.arange(E)
    c[:, C_HALF:C_HALF + 2 * MAXR] = np.arange(2 * MAXR) // 2
    c[:, C_HALF + 2 * MAXR:C_HALF + 4 * MAXR] = NSLOT * (np.arange(2 * MAXR) % 2)
    c[:, C_VALID] = p >= 31
    c[:, C_EXP:C_EXP + 8] = -0.5
    hot = np.zeros((33, ZLEN), np.float32)
    for z in range(ZLEN):
        n = S - 1 - z
        exact = NBUCKET // 2
        if n < 0:
            b = NBUCKET
        elif n < exact:
            b = n
        else:
            b = min(exact + int(math.log(n / exact) / math.log(128 / exact) * (NBUCKET - exact) + 1e-9), NBUCKET - 1)
        hot[b, z] = 1
    return c, hot


def kernel(**inputs):
    import concourse.bacc as bacc
    from concourse.bass_utils import run_bass_kernel_spmd

    a = {k: np.asarray(v) for k, v in inputs.items()}
    con, hot = shape_constants()
    w = a["w_in"].reshape(DEPTH, KD, P, -1).transpose(0, 2, 1, 3)
    o = 512
    kc, vc, ks, vs, kw, vw = (w[..., o + 128 * i:o + 128 * (i + 1)] for i in range(6))
    o += 768
    gates = w[..., o:o + 24]
    cb, cc, ch = (w[..., o + 24 + i * CW:o + 24 + (i + 1) * CW] for i in range(3))
    w_cv = np.stack([np.concatenate([m[..., c * P:(c + 1) * P] for m in (cb, cc, ch)], -1) for c in range(CT)], 1)
    w_1 = np.stack([a[n].reshape(DEPTH, LP, P, HID).transpose(0, 2, 1, 3) for n in ("cmp_k_w1", "cmp_v_w1")], 2)
    w_o = a["w_out"].reshape(DEPTH, KD, P, D).transpose(0, 2, 1, 3)
    n_b = np.stack([a["norm1"], a["norm2"]], 1).reshape(2 * DEPTH, D)
    p_b = np.concatenate([a["attn_out_norm"], a["q_norm"], a["k_norm"].reshape(DEPTH, -1)], 1)
    p_c = np.concatenate([
        a["conv_w"].reshape(DEPTH, 3, CT, P).transpose(0, 3, 2, 1).reshape(DEPTH, P, 3 * CT),
        a["conv_out_norm"].reshape(DEPTH, CT, P).transpose(0, 2, 1),
        a["cmp_pos_k"].reshape(DEPTH, LP, P).transpose(0, 2, 1), a["cmp_pos_v"].reshape(DEPTH, LP, P).transpose(0, 2, 1),
        a["cmp_k_w2"], a["cmp_v_w2"]], 2)

    def gate_up(g, u):
        t = [m.reshape(-1, KD, P, FT, P).transpose(0, 3, 2, 1, 4).reshape(-1, FT, P, KD * P) for m in (g, u)]
        return np.concatenate(t, -1)

    f_gu = gate_up(a["ffn_w_gate"], a["ffn_w_up"])[0]
    d = a["ffn_w_down"][0].reshape(2, NSLOT, P, D)
    f_dn = d.transpose(1, 2, 0, 3).reshape(NSLOT, P, 2 * D)
    m_w = np.concatenate([gate_up(a["moe_w_gate"][0], a["moe_w_up"][0]), a["moe_w_down"][0].reshape(E, FT, P, D)], -1)
    r_w = a["router_w"][0].reshape(KD, P, E).transpose(1, 0, 2)
    arrays = {
        "x_in": a["x"][0], "table": a["rel_bias"], "onehot": hot, "const": con,
        "w_q": w[..., 0:512], "w_kv": np.concatenate([ks, vs, kw, vw], -1), "w_kc": np.concatenate([kc, vc, gates], -1),
        "w_cv": w_cv, "w_1": w_1, "w_o": w_o, "n_b": n_b, "p_b": p_b, "p_c": p_c, "f_gu": f_gu, "f_dn": f_dn,
        "r_w": r_w, "r_b": a["router_b"], "m_w": m_w.reshape(E * FT, P, SLOT),
    }
    w_cv_t = arrays["w_cv"]
    arrays["w_cv"] = w_cv_t
    nc = bacc.Bacc("TRN2", target_bir_lowering=False, num_devices=1)
    feeds, args = {}, []
    for name, v in arrays.items():
        feeds[name] = np.ascontiguousarray(v)
        args.append(nc.dram_tensor(name, v.shape, mybir.dt.from_np(v.dtype), kind="ExternalInput").ap())
    args.append(nc.dram_tensor("out", (S, D), F32, kind="ExternalOutput").ap())
    build(nc, *args)
    r = run_bass_kernel_spmd(nc, [feeds], core_ids=[0])
    return r.results[0]["out"].reshape(1, S, D)
```
